# Optimizing a Trainium2 kernel written in Bass

```python
import jax, jax.numpy as jnp
from jax import lax
import numpy as np

D_MODEL = 1024
BATCH = 1
SEQ = 256
DEPTH = 1
DEC_BATCH = 8
DEC_SEQ = 1
PAST_LEN = 2048
PAGE_SIZE = 128

POOL_WIDTH = 1024
POOL_WINDOWS = (2, 4, 8, 16)
POOL_GROUPS = len(POOL_WINDOWS)
POOL_GROUP_WIDTH = POOL_WIDTH // POOL_GROUPS
POOL_BUF = max(POOL_WINDOWS) - 1
RET_HEADS = 4
RET_QK_DIM = D_MODEL // RET_HEADS
RET_V_DIM = 2 * D_MODEL // RET_HEADS
RET_QK_WIDTH = RET_HEADS * RET_QK_DIM
RET_V_WIDTH = RET_HEADS * RET_V_DIM
RET_CHUNK = 128
ROPE_BASE = 10000.0
IN_SIZES = (POOL_WIDTH, RET_QK_WIDTH, RET_QK_WIDTH, RET_V_WIDTH, RET_V_WIDTH, D_MODEL, D_MODEL)
IN_WIDTH = sum(IN_SIZES)
IN_SPLITS = tuple(int(s) for s in np.cumsum(IN_SIZES)[:-1])
N_EXPERTS = 32
TOP_K = 4
D_EXPERT = D_MODEL
SWIGLU_LIMIT = 7.0
SWIGLU_ALPHA = 1.702
N_MOD = 6
EPS = 1e-6

kernel_name = "pool_retention_moe_adaln_decode_step"

def rmsnorm(x, g=None):
    xf = x.astype(jnp.float32)
    y = xf * lax.rsqrt(jnp.mean(xf * xf, axis=-1, keepdims=True) + EPS)
    if g is not None:
        y = y * g.astype(jnp.float32)
    return y.astype(x.dtype)

def retention_log_decay():
    return jnp.log(1.0 - jnp.power(2.0, -5.0 - jnp.arange(RET_HEADS, dtype=jnp.float32)))

def rotary(x, pos):
    half = x.shape[-1] // 2
    inv = jnp.power(ROPE_BASE, -jnp.arange(half, dtype=jnp.float32) / half)
    ang = pos.astype(jnp.float32)[:, None] * inv[None, :]
    cos, sin = jnp.cos(ang), jnp.sin(ang)
    x1, x2 = x[..., :half], x[..., half:]
    return jnp.concatenate([x1 * cos - x2 * sin, x2 * cos + x1 * sin], axis=-1)

def pool_mixer(u, buf, pos0, w_pool, pool_scale):
    T = u.shape[1]
    L = POOL_BUF
    ext = jnp.concatenate([buf.astype(jnp.float32), u.astype(jnp.float32)], axis=1)
    cs = jnp.concatenate([jnp.zeros_like(ext[:, :1]), jnp.cumsum(ext, axis=1)], axis=1)
    end = cs[:, L + 1:L + 1 + T]
    pos = pos0 + jnp.arange(T, dtype=jnp.int32)
    outs = []
    for gi, w in enumerate(POOL_WINDOWS):
        sl = slice(gi * POOL_GROUP_WIDTH, (gi + 1) * POOL_GROUP_WIDTH)
        start = cs[:, L + 1 - w:L + 1 - w + T, sl]
        cnt = jnp.minimum(w, pos + 1).astype(jnp.float32)[None, :, None]
        pooled = (end[..., sl] - start) / cnt - ext[:, L:, sl]
        outs.append(jnp.einsum('btc,cd->btd', pooled, w_pool[gi].astype(jnp.float32)))
    y = jnp.concatenate(outs, axis=-1) * pool_scale.astype(jnp.float32)
    new_buf = ext[:, -L:]
    return y.astype(u.dtype), new_buf

def retention_block(q, k, v, S, log_gamma):
    C = q.shape[2]
    i = jnp.arange(C, dtype=jnp.float32)
    diff = i[:, None] - i[None, :]
    lg = log_gamma[:, None, None]
    decay = jnp.where(diff[None] >= 0, jnp.exp(lg * jnp.maximum(diff, 0.0)[None]), 0.0)
    scores = jnp.einsum('bhid,bhjd->bhij', q, k) * decay[None]
    q_dec = q * jnp.exp(log_gamma[:, None] * (i + 1.0)[None])[None, :, :, None]
    o = jnp.einsum('bhij,bhjv->bhiv', scores, v) + jnp.einsum('bhid,bhdv->bhiv', q_dec, S)
    k_dec = k * jnp.exp(log_gamma[:, None] * (C - 1.0 - i)[None])[None, :, :, None]
    S_new = jnp.exp(log_gamma * C)[None, :, None, None] * S + jnp.einsum('bhjd,bhjv->bhdv', k_dec, v)
    return o, S_new

def retention(q, k, v, S0, log_gamma):
    B, H, T, _ = q.shape
    C = RET_CHUNK if T % RET_CHUNK == 0 else T
    NC = T // C

    def to_chunks(a):
        return jnp.moveaxis(a.reshape(B, H, NC, C, a.shape[-1]), 2, 0)

    def step(S, qkv):
        qc, kc, vc = qkv
        o, S = retention_block(qc, kc, vc, S, log_gamma)
        return S, o

    S, o = lax.scan(step, S0, (to_chunks(q), to_chunks(k), to_chunks(v)))
    o = jnp.moveaxis(o, 0, 2).reshape(B, H, T, -1)
    return o, S

def token_mixer(h, pool_buf, ret_state, pos0, w_in, w_pool, pool_scale, w_up_pool, w_up_ret, w_out):
    B, T, _ = h.shape
    proj = h @ w_in
    u, q, k, v, g_ret, g_a, g_b = jnp.split(proj, IN_SPLITS, axis=-1)
    y_a, new_buf = pool_mixer(u, pool_buf, pos0, w_pool, pool_scale)
    pos = pos0 + jnp.arange(T, dtype=jnp.int32)

    def heads(a, d):
        return jnp.transpose(a.astype(jnp.float32).reshape(B, T, RET_HEADS, d), (0, 2, 1, 3))

    qh = rotary(heads(q, RET_QK_DIM), pos)
    kh = rotary(heads(k, RET_QK_DIM), pos) * (RET_QK_DIM ** -0.5)
    vh = heads(v, RET_V_DIM)
    o, S_new = retention(qh, kh, vh, ret_state.astype(jnp.float32), retention_log_decay())
    o = rmsnorm(o)
    o = jnp.transpose(o, (0, 2, 1, 3)).reshape(B, T, RET_V_WIDTH)
    y_b = (jax.nn.silu(g_ret.astype(jnp.float32)) * o).astype(h.dtype)
    merged = jax.nn.sigmoid(g_a) * (y_a @ w_up_pool) + jax.nn.sigmoid(g_b) * (y_b @ w_up_ret)
    return merged @ w_out, new_buf, S_new

def moe(h, w_router, b_router, w_expert_in, b_expert_in, w_expert_out, b_expert_out):
    B, T, D = h.shape
    xf = h.reshape(B * T, D)
    logits = (xf @ w_router + b_router).astype(jnp.float32)
    top_val, top_idx = lax.top_k(logits, TOP_K)
    top_w = jax.nn.softmax(top_val, axis=-1)
    comb = jnp.sum(jax.nn.one_hot(top_idx, N_EXPERTS, dtype=jnp.float32) * top_w[..., None], axis=1)
    y = jnp.zeros((B * T, D), jnp.float32)
    for e in range(N_EXPERTS):
        hh = (xf @ w_expert_in[e] + b_expert_in[e]).astype(jnp.float32)
        gate = jnp.minimum(hh[:, :D_EXPERT], SWIGLU_LIMIT)
        lin = jnp.clip(hh[:, D_EXPERT:], -SWIGLU_LIMIT, SWIGLU_LIMIT)
        act = ((lin + 1.0) * gate * jax.nn.sigmoid(SWIGLU_ALPHA * gate)).astype(h.dtype)
        y = y + comb[:, e:e + 1] * (act @ w_expert_out[e] + b_expert_out[e]).astype(jnp.float32)
    return y.astype(h.dtype).reshape(B, T, D)

def layer(x, c, pool_buf, ret_state, pos0, w_ada, b_ada, norm1_g, w_in, w_pool, pool_scale,
          w_up_pool, w_up_ret, w_out, norm2_g, w_router, b_router,
          w_expert_in, b_expert_in, w_expert_out, b_expert_out):
    mod = jax.nn.silu(c) @ w_ada + b_ada
    sh1, sc1, gt1, sh2, sc2, gt2 = jnp.split(mod[:, None, :], N_MOD, axis=-1)
    h = rmsnorm(x, norm1_g) * (1.0 + sc1) + sh1
    mix, new_buf, new_state = token_mixer(h, pool_buf, ret_state, pos0, w_in, w_pool, pool_scale,
                                          w_up_pool, w_up_ret, w_out)
    x = x + gt1 * mix
    h = rmsnorm(x, norm2_g) * (1.0 + sc2) + sh2
    x = x + gt2 * moe(h, w_router, b_router, w_expert_in, b_expert_in, w_expert_out, b_expert_out)
    return x, new_buf, new_state

def setup_inputs(seed: int = 0) -> dict:
    key = jax.random.key(seed)
    ks = jax.random.split(key, 24)
    f32 = jnp.float32
    D, E, F = D_MODEL, N_EXPERTS, D_EXPERT

    def nrm(k, shape, scale):
        return jax.random.normal(k, shape, f32) * scale

    return {
        "x_prompt": nrm(ks[0], (BATCH, SEQ, D), 1.0),
        "x_sample": nrm(ks[1], (DEC_BATCH, DEC_SEQ, D), 1.0),
        "c_prompt": nrm(ks[2], (BATCH, D), 1.0),
        "c_sample": nrm(ks[3], (DEC_BATCH, D), 1.0),
        "state_pool": nrm(ks[4], (DEPTH, DEC_BATCH, POOL_BUF, POOL_WIDTH), 1.0),
        "state_ret": nrm(ks[5], (DEPTH, DEC_BATCH, RET_HEADS, RET_QK_DIM, RET_V_DIM), 1.0),
        "w_ada": nrm(ks[6], (DEPTH, D, N_MOD * D), 0.5 * D ** -0.5),
        "b_ada": nrm(ks[7], (DEPTH, N_MOD * D), 0.02),
        "norm1_g": 1.0 + nrm(ks[8], (DEPTH, D), 0.1),
        "w_in": nrm(ks[9], (DEPTH, D, IN_WIDTH), D ** -0.5),
        "w_pool": nrm(ks[10], (DEPTH, POOL_GROUPS, POOL_GROUP_WIDTH, POOL_GROUP_WIDTH), POOL_GROUP_WIDTH ** -0.5),
        "pool_scale": 1.0 + nrm(ks[11], (DEPTH, POOL_WIDTH), 0.1),
        "w_up_pool": nrm(ks[12], (DEPTH, POOL_WIDTH, D), POOL_WIDTH ** -0.5),
        "w_up_ret": nrm(ks[13], (DEPTH, RET_V_WIDTH, D), RET_V_WIDTH ** -0.5),
        "w_out": nrm(ks[14], (DEPTH, D, D), D ** -0.5),
        "norm2_g": 1.0 + nrm(ks[15], (DEPTH, D), 0.1),
        "w_router": nrm(ks[16], (DEPTH, D, E), D ** -0.5),
        "b_router": nrm(ks[17], (DEPTH, E), 0.01),
        "w_expert_in": nrm(ks[18], (DEPTH, E, D, 2 * F), D ** -0.5),
        "b_expert_in": nrm(ks[19], (DEPTH, E, 2 * F), 0.01),
        "w_expert_out": nrm(ks[20], (DEPTH, E, F, D), F ** -0.5),
        "b_expert_out": nrm(ks[21], (DEPTH, E, D), 0.01),
        "final_norm_g": 1.0 + nrm(ks[22], (D,), 0.1),
    }

def reference(x_prompt, x_sample, c_prompt, c_sample, state_pool, state_ret,
              w_ada, b_ada, norm1_g, w_in, w_pool, pool_scale, w_up_pool, w_up_ret, w_out,
              norm2_g, w_router, b_router, w_expert_in, b_expert_in, w_expert_out, b_expert_out,
              final_norm_g):
    xp, xs = x_prompt, x_sample
    pool_p, ret_p, pool_s, ret_s = [], [], [], []
    for l in range(DEPTH):
        weights = (w_ada[l], b_ada[l], norm1_g[l], w_in[l], w_pool[l], pool_scale[l],
                   w_up_pool[l], w_up_ret[l], w_out[l], norm2_g[l], w_router[l], b_router[l],
                   w_expert_in[l], b_expert_in[l], w_expert_out[l], b_expert_out[l])
        buf0 = jnp.zeros((xp.shape[0], POOL_BUF, POOL_WIDTH), jnp.float32)
        S0 = jnp.zeros((xp.shape[0], RET_HEADS, RET_QK_DIM, RET_V_DIM), jnp.float32)
        xp, nb_p, ns_p = layer(xp, c_prompt, buf0, S0, 0, *weights)
        xs, nb_s, ns_s = layer(xs, c_sample, state_pool[l], state_ret[l], PAST_LEN, *weights)
        pool_p.append(nb_p.astype(x_prompt.dtype))
        ret_p.append(ns_p.astype(x_prompt.dtype))
        pool_s.append(nb_s.astype(state_pool.dtype))
        ret_s.append(ns_s.astype(state_ret.dtype))
    y_prompt = rmsnorm(xp, final_norm_g)
    y_sample = rmsnorm(xs, final_norm_g)
    new_pool_prompt = jnp.stack(pool_p, axis=0)
    new_ret_prompt = jnp.stack(ret_p, axis=0)
    new_pool_sample = jnp.stack(pool_s, axis=0)
    new_ret_sample = jnp.stack(ret_s, axis=0)
    return (y_prompt, y_sample, new_pool_prompt, new_ret_prompt, new_pool_sample, new_ret_sample)


_drawn_inputs = setup_inputs


def setup_inputs(seed=0):
    import zlib

    import numpy as np

    out = dict(_drawn_inputs(seed))
    spreads = {}
    factors = {'pool_scale': 2.763, 'b_router': 7.716, 'b_expert_in': 29.991, 'b_expert_out': 36.611}
    for name, (base, spread) in spreads.items():
        noise = np.random.default_rng([zlib.crc32(name.encode()), seed]).standard_normal(out[name].shape)
        drawn = base * np.exp(spread * noise) if base else spread * noise
        out[name] = __import__('jax').numpy.asarray(drawn.astype(out[name].dtype))
    for name, factor in factors.items():
        out[name] = (out[name] * factor).astype(out[name].dtype)
    return out
```

```python
from contextlib import ExitStack

import numpy as np

import concourse.bass as bass
from concourse import mybir

F32 = mybir.dt.float32
F32R = mybir.dt.float32r
BF16 = mybir.dt.bfloat16
U32 = mybir.dt.uint32
I32 = mybir.dt.int32
ALU = mybir.AluOpType
ACT = mybir.ActivationFunctionType
AX = mybir.AxisListType.X

P = 128
D = 1024
KC = D // P
TP, TS = 256, 8
T = TP + TS
NB = 1 + TS
COL = 512
HEADS, QK, VD = 4, 256, 512
IN_W = 9 * D
NCH = IN_W // P
U0, Q0, K0, V0, G0, GA0, GB0 = 0, 8, 16, 24, 40, 56, 64
WINDOWS = (2, 4, 8, 16)
BUF = 15
E = 32
TOPK = 4
LIMIT, ALPHA, EPS = 7.0, 1.702, 1e-6
PAST = 2048
ADA_BLOCKS = 6 * D // COL
IN_BLOCKS = IN_W // COL
RING = 3
PAD = 16
EXT = PAD + TP
POOL_GW = D // len(WINDOWS)
SMALL_LOADS = 9
SKIP = 4096.0
GAMMA = [float(np.exp(np.log(np.float32(1) - np.float32(2) ** np.float32(-5 - h)))) for h in range(HEADS)]
TILES = [(0, P), (P, P), (TP, TS)]

CONST = {}
_at = 0
for _name, _w in [("ident", P), ("iota", P), ("selc", T), ("tokv", 4), ("eye96", 36),
                  ("ones", P), ("upper", P), ("cos", T), ("sin", T), ("decay", HEADS * TP), ("kdecay", 2 * HEADS),
                  ("sel", TS * P), ("eye8", TS * TS), ("cntinv", 4 * TP)]:
    CONST[_name] = (_at, _w)
    _at += _w
CONST_W = _at


def constant_table():
    t = np.zeros((P, CONST_W), np.float32)

    def put(name, a):
        a = np.asarray(a, np.float32).reshape(a.shape[0], -1)
        t[:a.shape[0], CONST[name][0]:CONST[name][0] + a.shape[1]] = a

    pos = np.concatenate([np.arange(TP), np.full(TS, PAST)]).astype(np.float32)
    inv = np.power(np.float32(10000.0), -np.arange(P, dtype=np.float32) / np.float32(P)).astype(np.float32)
    ang = (inv[:, None] * pos[None, :]).astype(np.float32)
    put("cos", np.cos(ang))
    put("sin", np.sin(ang))
    lg = np.log(1.0 - 2.0 ** (-5.0 - np.arange(HEADS)))
    j, i = np.arange(P)[:, None], np.arange(TP)[None, :]
    put("decay", np.stack([np.where(i >= j, np.exp(g * np.maximum(i - j, 0)), 0.0) for g in lg], 1))
    put("kdecay", np.stack([np.exp(g * (TP - 1 - (np.arange(P) + P * a))) for a in range(2) for g in lg], 1))
    put("ident", np.eye(P))
    put("upper", np.triu(np.ones((P, P)), 1))
    put("ones", np.ones((P, P)))
    put("sel", np.repeat(np.eye(TS)[:, :, None], P, 2))
    put("eye8", np.tile(np.eye(TS).reshape(1, -1), (P, 1)))
    put("iota", np.tile(np.arange(P), (P, 1)))
    put("cntinv", np.tile(np.stack([1.0 / np.minimum(w, np.arange(TP) + 1) for w in WINDOWS]).reshape(1, -1), (P, 1)))
    put("selc", np.concatenate([np.eye(NB)[:, :1].repeat(TP, 1), np.eye(NB)[:, 1:]], 1))
    put("tokv", np.arange(P)[:, None] + P * np.arange(4)[None, :])
    put("eye96", np.tile(np.eye(E), (3, 1)))
    return t


def trunk_kernel(nc, x_prompt, x_sample, c_prompt, c_sample, state_pool, state_ret, w_ada, b_ada, norm1_g, w_in,
                 w_pool, pool_scale, w_up_pool, w_up_ret, w_out, norm2_g, w_router, b_router, w_expert_in,
                 b_expert_in, w_expert_out, b_expert_out, final_norm_g, consts,
                 y_prompt, y_sample, new_pool_prompt, new_ret_prompt, new_pool_sample, new_ret_sample):
    h2_rows = nc.dram_tensor("h2_rows", (T, D), F32, kind="Internal").ap()
    x1_rows = nc.dram_tensor("x1_rows", (T, D), F32, kind="Internal").ap()
    expert_rows = nc.dram_tensor("expert_rows", (T * TOPK, D), F32, kind="Internal").ap()

    ctx = ExitStack()
    with ctx:
        top = [(nc.sbuf_base + 63) // 64 * 64]

        def at(name, shape, offset, dt=F32):
            return nc.alloc_sbuf_tensor_at(name, shape, dt, offset=offset)

        def size(shape, dt=F32):
            return (int(np.prod(shape[1:])) * (2 if dt == BF16 else 4) + 31) // 32 * 32

        def new(name, shape, dt=F32):
            t = at(name, shape, top[0], dt)
            top[0] += size(shape, dt)
            return t

        dead_at = top[0] + 4 * CONST["ones"][0]
        ct = new("ct", [P, CONST_W])
        xT = new("xT", [P, KC, T])
        vecT = new("vecT", [P, 72])
        modT = new("modT", [P, 48, NB])
        scale1 = new("scale1", [P, KC, NB])
        scale2 = new("scale2", [P, KC, NB])
        rstd = new("rstd", [P, T])
        sq = new("sq", [P, 2, T])
        u_tail = new("u_tail", [P, KC, BUF + TS])
        outer_sum = new("outer_sum", [P, KC, TS])
        dead_end = top[0]
        ring = [new(f"ring{s}", [P, KC, COL]) for s in range(RING)]
        work = top[0]
        projT = new("projT", [P, NCH, T])
        h_at = top[0]
        hT = new("hT", [P, KC, T])
        v_at = top[0]
        vtok = new("vtok", [P, 3, HEADS * VD])
        misc = top[0]
        top[0] += 2 * 4096
        scoresT = new("scoresT", [P, 2, TP + P])
        s_stage = new("s_stage", [P, 2, VD])
        q_mask = new("q_mask", [P, 2 * HEADS, TS, TS])
        assert top[0] <= nc.sbuf_usable_end, (top[0], nc.sbuf_usable_end)
        xtok = at("xtok", [P, 3, D], v_at)
        rows72 = at("rows72", [72, P], v_at + 12288)
        crow = at("crow", [NB, D], v_at + 12800)
        csil = at("csil", [NB, D], v_at + 16896)
        cT = at("cT", [P, KC, NB], v_at + 20992)
        ext = at("ext", [P, KC, EXT], v_at)
        sum2 = at("sum2", [P, KC, EXT], v_at + size([P, KC, EXT]))
        sum4 = at("sum4", [P, 6, EXT], v_at + 2 * size([P, KC, EXT]))
        o_rows = at("o_rows", [TS, HEADS * VD], v_at)
        o_sq = at("o_sq", [P, 4, T], v_at + 8192)
        up_a = at("up_a", [P, T], v_at + 12544)
        up_b = at("up_b", [P, T], v_at + 13696)
        mod_stage = at("mod_stage", [NB, RING, COL], work)
        spool = at("spool", [TS * BUF, D], h_at)
        rot_a = at("rot_a", [P, HEADS, T], h_at)
        rot_b = at("rot_b", [P, HEADS, T], h_at + size([P, HEADS, T]))
        kdec = at("kdec", [P, 2, D], h_at)
        extS = at("extS", [P, KC, TS, 16], misc)
        u_rows = at("u_rows", [BUF + TS, D], misc + 4096)
        outer = at("outer", [P, 2, 2, VD], misc)
        mergedT = projT[:, K0:K0 + KC, :]

        top[0] = work
        moe_ring = list(ring) + [new(f"moe_ring{s}", [P, KC, COL]) for s in range(3, 6)]
        moe_ring_at = [dead_end + s * size([P, KC, COL]) for s in range(6)]
        moe5_at = top[0] - size([P, KC, COL])
        xg_at = top[0]
        xg = new("xg", [P, D])
        xgT_at = top[0]
        xgT_hi = new("xgT_hi", [P, 2, KC, P], F32R)
        xgT_lo = new("xgT_lo", [P, 2, KC, P], F32R)
        w_hi = [at(f"w_hi{i}", [P, KC // 2, COL], dead_at + i * size([P, KC // 2, COL]), F32R) for i in range(3)]
        assert dead_at + 3 * size([P, KC // 2, COL]) <= dead_end
        w_hi.append(new("w_hi3", [P, KC // 2, COL], F32R))
        w_lo = [at(f"w_lo{s}", [P, KC, COL], moe_ring_at[s], F32R) for s in range(4)]
        actT = new("actT", [P, KC, P])
        act_at = top[0]
        act = new("act", [P, 2, COL])
        glu_g = new("glu_g", [P, COL])
        glu_l = new("glu_l", [P, COL])
        glu_s = new("glu_s", [P, COL])
        ostage_at = top[0]
        ostage = new("ostage", [P, 2, D])
        bsplit = new("bsplit", [96, 2 * D], BF16)
        picked = new("picked", [P, 3, P])
        bias_sel = new("bias_sel", [96, 2, P], BF16)
        slot_v = new("slot_v", [P, 3, E + 1, 3])
        rankm = new("rankm", [P, 3, E + 1])
        slot_new = new("slot_new", [P, 3])
        slot_t = new("slot_t", [P, 1], U32)
        slot_u = new("slot_u", [P, 2, 1], U32)
        slot_w = new("slot_w", [P, 2, 1])
        routew = new("routew", [P, KC, E])
        rbias = new("rbias", [P, E])
        logits = new("logits", [P, E])
        top8 = new("top8", [P, 8])
        idx8 = new("idx8", [P, 8], U32)
        idxf = new("idxf", [P, 8])
        wk = new("wk", [P, 8])
        small = new("small", [P, 16])
        combt = new("combt", [P, 3, E])
        maskt = new("maskt", [P, 3, E])
        kt = new("kt", [P, 3, E])
        onehot = new("onehot", [P, E])
        rounds_f = new("rounds_f", [P, 2])
        rounds_i = new("rounds_i", [P, 1], I32)
        countf = new("countf", [P, E])
        combT = new("combT", [E, T])
        gate_rows = new("gate_rows", [NB, D])
        assert top[0] <= nc.sbuf_usable_end, (top[0], nc.sbuf_usable_end)
        h2T = at("h2T", [P, KC, T], xgT_at)
        rows = at("rows", [P, 3, D], act_at)
        b_full = at("b_full", [96, 2 * D], moe5_at)
        b_part = at("b_part", [96, 2 * D], moe5_at + 8192)
        b_half = at("b_half", [96, 2 * D], xg_at, BF16)
        x1_rows_in = at("x1_rows_in", [P, 3, D], moe_ring_at[3])
        b_out = at("b_out", [E, D], xg_at)
        g_final = at("g_final", [P, D], xgT_at)
        y_out = [at(f"y_out{t}", [P, D], ostage_at + 4096 * t) for t in range(2)] + [at("y_out2", [P, D], xgT_at + 4096)]
        y_sq = at("y_sq", [P, D], xgT_at + 8192)

        ps = ctx.enter_context(nc.psum_tensor("ps", [P, 8, 512], F32))

        def const(name, rows=P):
            a, w = CONST[name]
            return ct[0:rows, a:a + w]

        ident = const("ident")
        ones = const("ones")

        def over(ap, n):
            return ap.unsqueeze(1).broadcast_to([ap.shape[0], n, ap.shape[1]])

        def each(ap, n):
            return ap.unsqueeze(2).broadcast_to([ap.shape[0], ap.shape[1], n])

        def sem(name):
            return ctx.enter_context(nc.semaphore(name))

        const_in, small_in = sem("const_in"), sem("small_in")
        loaded = [sem(f"loaded{s}") for s in range(RING)]
        vec_turned, vec_copied = sem("vec_turned"), sem("vec_copied")
        x_turned, x_copied = sem("x_turned"), sem("x_copied")
        c_silu, c_turned, c_copied = sem("c_silu"), sem("c_turned"), sem("c_copied")
        pool_turned, pool_copied = sem("pool_turned"), sem("pool_copied")
        sq_ready, sq_summed = sem("sq_ready"), sem("sq_summed")
        var_ready, std_ready = sem("var_ready"), sem("std_ready")
        ada_ready, ada_staged, ada_turned, mod_ready = sem("ada_ready"), sem("ada_staged"), sem("ada_turned"), sem("mod_ready")
        normed, h_ready = sem("normed"), sem("h_ready")
        in_ready = [sem(f"in_ready{j}") for j in range(4)]
        in_taken = [sem(f"in_taken{j}") for j in range(4)]
        pool_step, pool_done = sem("pool_step"), sem("pool_done")
        tail_turned, tail_copied, tail_stored = sem("tail_turned"), sem("tail_copied"), sem("tail_stored")
        v_turned, v_copied = sem("v_turned"), sem("v_copied")
        k_rotated, q_rotated, mask_ready = sem("k_rotated"), sem("q_rotated"), sem("mask_ready")
        k_turned, k_copied = sem("k_turned"), sem("k_copied")
        scored, score_taken = sem("scored"), sem("score_taken")
        o_ready, o_taken = sem("o_ready"), sem("o_taken")
        state_ready, state_taken, state_stored = sem("state_ready"), sem("state_taken"), [sem("state_stored0"), sem("state_stored1")]
        v_spread, outer_ready, s_updated = sem("v_spread"), sem("outer_ready"), sem("s_updated")
        so_done, s_stored = sem("so_done"), [sem(f"s_stored{s}") for s in range(RING)]
        so_rows, so_turned, so_copied = sem("so_rows"), sem("so_turned"), sem("so_copied")
        gates_ready, o_squared, o_summed = sem("gates_ready"), sem("o_squared"), sem("o_summed")
        o_var, o_std, o_normed = sem("o_var"), sem("o_std"), sem("o_normed")
        pooled_s = sem("pooled_s")
        mix_ready, mix_taken = sem("mix_ready"), sem("mix_taken")
        up_ready, up_taken = sem("up_ready"), sem("up_taken")
        out_ready, x1_ready = sem("out_ready"), sem("x1_ready")
        dve_step = sem("dve_step")
        x1_turned, h2_turned, h2_stored, x1_stored = sem("x1_turned"), sem("h2_turned"), sem("h2_stored"), sem("x1_stored")
        hi_ready, lo_ready, half_used, xg_hi = sem("hi_ready"), sem("lo_ready"), sem("half_used"), sem("xg_hi")
        x1_copied = [sem("x1_copied0"), sem("x1_copied1")]
        h2_copied = [sem("h2_copied0"), sem("h2_copied1")]
        route_in, bias_in, logit_ready, mask_sum = sem("route_in"), sem("bias_in"), sem("logit_ready"), sem("mask_sum")
        routes_ready, exp_in, exp_out, ranked = sem("routes_ready"), sem("exp_in"), sem("exp_out"), sem("ranked")
        prep_ready, comb_turned, bias_split = sem("prep_ready"), sem("comb_turned"), sem("bias_split")
        moe_loaded = [sem(f"moe_loaded{s}") for s in range(6)]
        picked_ready, slots_ready, slots_taken = sem("picked_ready"), sem("slots_ready"), sem("slots_taken")
        slots_settled = sem("slots_settled")
        bias_sel_ready, xg_loaded, xg_turned, xg_taken = sem("bias_sel_ready"), sem("xg_loaded"), sem("xg_turned"), sem("xg_taken")
        hidden_ready, glu_ready, sig_ready, act_ready = sem("hidden_ready"), sem("glu_ready"), sem("sig_ready"), sem("act_ready")
        act_turned, act_taken = sem("act_turned"), sem("act_taken")
        eo_ready, eo_taken, eo_stored, rows_free = sem("eo_ready"), sem("eo_taken"), sem("eo_stored"), sem("rows_free")
        moe_step, pool_pace, rank_step = sem("moe_step"), sem("pool_pace"), sem("rank_step")
        pe_pace = sem("pe_pace")
        rows_in, bo_ready, y_step = sem("rows_in"), sem("bo_ready"), sem("y_step")
        gates_turned, y_sumsq, y_std, y_ready, y_stored = sem("gates_turned"), sem("y_sumsq"), sem("y_std"), sem("y_ready"), sem("y_stored")

        block = ctx.enter_context(nc.Block())

        @block.sync
        def _(sp):
            def columns(w, c):
                return w.rearrange("(k p) n -> p k n", p=P)[:, :, c * COL:(c + 1) * COL]

            def columns_at(w, c):
                return w.rearrange("(k p) n -> p k n", p=P)[:, :, bass.ds(c * COL, COL)]

            sp.wait_ge(small_in, 16 * SMALL_LOADS)
            with sp.Fori(0, ADA_BLOCKS // RING) as i:
                for s in range(RING):
                    sp.wait_ge(ada_ready, i * RING + (s + 1))
                    sp.dma_start(ring[s][:], columns_at(w_ada[0], i * RING + s)).then_inc(loaded[s], 16)
            for s in range(RING):
                sp.wait_ge(ada_ready, ADA_BLOCKS + 1 + s)
                sp.dma_start(ring[s][:], columns(w_in[0], s)).then_inc(loaded[s], 16)
            with sp.Fori(1, IN_BLOCKS // RING) as i:
                for s in range(RING):
                    sp.wait_ge(in_ready[3], i * RING + (s - 2))
                    sp.dma_start(ring[s][:], columns_at(w_in[0], i * RING + s)).then_inc(loaded[s], 16)
            for b in range(TS):
                s = b % RING
                if b < RING:
                    sp.wait_ge(in_ready[3], IN_BLOCKS - RING + 1 + b)
                else:
                    sp.wait_ge(s_stored[s], 16 * (b // RING))
                    sp.wait_ge(so_done, HEADS * (b - RING + 1))
                sp.dma_start(ring[s][:], state_ret[0, b].rearrange("h (c p) v -> p (h c) v", p=P)).then_inc(loaded[s], 16)
            late = [("pool", w_pool[0].rearrange("g (c p) n -> p (g c) n", p=P))]
            for c in range(2):
                late.append(("up", columns(w_up_pool[0], c)))
                for r in range(2):
                    late.append(("up", columns(w_up_ret[0, r * D:(r + 1) * D], c)))
            late += [("out", columns(w_out[0], c)) for c in range(2)]
            freed = {3: (mix_ready, KC), 4: (up_ready, 4), 5: (up_ready, 4), 6: (up_ready, 4), 7: (up_ready, 8), 8: (up_ready, 8)}
            for j, (kind, src) in enumerate(late):
                n = TS + j
                s = n % RING
                if j < RING:
                    sp.wait_ge(s_stored[s], 16 * (n // RING))
                    sp.wait_ge(so_done, HEADS * (n - RING + 1))
                else:
                    sp.wait_ge(*freed[j])
                dst = ring[s][:]
                if kind == "pool":
                    dst = ring[s][:].rearrange("p k n -> p (k n)")[:, 0:KC * POOL_GW].rearrange("p (k n) -> p k n", n=POOL_GW)
                sp.dma_start(dst, src).then_inc(loaded[s], 16)

            def hidden(s, q, e):
                c = (0, 2, 1, 3)[s]
                sp.wait_ge(hidden_ready, 4 * q + (s + 5))
                sp.dma_start(moe_ring[s][:], columns(w_expert_in[0, bass.ds(e, 1)].rearrange("a k n -> (a k) n"), c)).then_inc(moe_loaded[s], 16)

            def outward(h, m, e):
                if h == 1:
                    sp.wait_ge(bias_split, 1)
                sp.wait_ge(eo_ready, 2 * m + (h + 1))
                sp.dma_start(moe_ring[4 + h][:], columns(w_expert_out[0, bass.ds(e, 1)].rearrange("a k n -> (a k) n"), h)).then_inc(moe_loaded[4 + h], 16)

            sp.wait_ge(out_ready, KC)
            sp.wait_ge(x1_ready, KC)
            for s in range(4):
                hidden(s, 0, 0)
            sp.wait_ge(routes_ready, 1)
            rounds = sp.value_load(rounds_i[0:1, 0:1], min_val=1, max_val=3)
            with sp.Fori(0, rounds) as r:
                with sp.Fori(0, E - 1) as i:
                    for s in (0, 1):
                        hidden(s, r * E + i + 1, i + 1)
                    for h in (0, 1):
                        outward(h, r * E + i, i)
                    for s in (2, 3):
                        hidden(s, r * E + i + 1, i + 1)
                outward(0, r * E + (E - 1), E - 1)
                outward(1, r * E + (E - 1), E - 1)
                with sp.If(r + 1 < rounds):
                    for s in range(4):
                        hidden(s, r * E + E, 0)
            sp.wait_ge(rows_free, rounds * E + 2)
            sp.wait_ge(hidden_ready, rounds * (4 * E) + 8)
            sp.dma_start(x1_rows_in[:, 0:2, :], x1_rows[0:TP].rearrange("(t p) d -> p t d", p=P)).then_inc(rows_in, 16)
            sp.dma_start(x1_rows_in[0:TS, 2, :], x1_rows[TP:T]).then_inc(rows_in, 16)
            for t, (t0, n) in enumerate(TILES):
                sp.dma_start(ring[t][0:n].rearrange("p k n -> p (k n)"),
                             expert_rows[t0 * TOPK:(t0 + n) * TOPK].rearrange("(p k) n -> p (k n)", k=TOPK)).then_inc(rows_in, 16)
            for t, (t0, n) in enumerate(TILES):
                sp.wait_ge(y_ready, t + 1)
                dst = y_prompt[0, t0:t0 + n] if t < 2 else y_sample[:, 0]
                sp.dma_start(dst, y_out[t][0:n]).then_inc(y_stored, 16)
            sp.wait_ge(y_stored, 48)
            sp.wait_ge(tail_stored, 48)
            for par in range(2):
                sp.wait_ge(state_stored[par], 16 * HEADS)
            for s in range(RING):
                sp.wait_ge(s_stored[s], 16 * len(range(s, TS, RING)))

        @block.tensor
        def _(pe):
            def turn(out, in_):
                return nc.tensor.transpose(out, in_, ident[0:in_.shape[0], 0:in_.shape[0]])

            pe.sem_inc(ada_ready, 3)
            pe.sem_inc(hidden_ready, 8)
            pe.sem_inc(eo_ready, 2)
            pe.sem_inc(xg_turned, 2)
            pe.sem_inc(half_used, 4)
            pe.wait_ge(const_in, 16)
            pe.wait_ge(small_in, 16 * SMALL_LOADS)
            turn(ps[:, 6, 0:72], rows72[:]).then_inc(vec_turned, 1)
            for k in range(KC):
                if k >= 2:
                    pe.wait_ge(x_copied, k - 1)
                for t, (t0, n) in enumerate(TILES):
                    mm = turn(ps[:, k % 2, t0:t0 + n], xtok[0:n, t, k * P:(k + 1) * P])
                mm.then_inc(x_turned, 1)
            for g in range(2):
                for k in range(4):
                    mm = turn(ps[:, 2 + g, k * 120:(k + 1) * 120], spool[:, (4 * g + k) * P:(4 * g + k + 1) * P])
                mm.then_inc(pool_turned, 1)
            pe.wait_ge(c_silu, 1)
            for k in range(KC):
                mm = turn(ps[:, 7, k * NB:(k + 1) * NB], csil[:, k * P:(k + 1) * P])
            mm.then_inc(c_turned, 1)

            def sum_squares(base):
                for k in range(KC):
                    pe.wait_ge(sq_ready, base + k + 1)
                    nc.tensor.matmul(ps[:, 6, 0:T], ones, sq[:, k % 2, :], start=(k == 0), stop=(k == KC - 1)).then_inc(sq_summed, 1)

            pe.wait_ge(vec_copied, 1)
            sum_squares(0)
            pe.wait_ge(c_copied, 1)
            pe.wait_ge(x_copied, KC)
            pe.wait_ge(pool_copied, 2)
            with pe.Fori(0, ADA_BLOCKS // RING) as i:
                for s in range(RING):
                    pe.wait_ge(loaded[s], i * 16 + 16)
                    for k in range(KC):
                        mm = nc.tensor.matmul(ps[0:NB, s, :], cT[:, k, :], ring[s][:, k, :], start=(k == 0), stop=(k == KC - 1))
                    mm.then_inc(ada_ready, 1)
                for s in range(RING):
                    pe.wait_ge(ada_staged, i * RING + (s + 1))
                    pe.wait_ge(mod_ready, i * RING + (s + 1))
                    pe.sem_inc(pe_pace, 1)
                    for j in range(4):
                        mm = turn(ps[:, 3 + s, j * NB:(j + 1) * NB], mod_stage[:, s, j * P:(j + 1) * P])
                    mm.then_inc(ada_turned, 1)
            pe.wait_ge(h_ready, KC + 1)
            with pe.Fori(0, IN_BLOCKS // RING) as i:
                for s in range(RING):
                    pe.wait_ge(loaded[s], i * 16 + (ADA_BLOCKS // RING + 1) * 16)
                    for j in range(4):
                        pe.wait_ge(in_taken[j], i * RING + (s + 1))
                        for k in range(KC):
                            mm = nc.tensor.matmul(ps[:, j, 0:T], ring[s][:, k, j * P:(j + 1) * P], hT[:, k, :], start=(k == 0), stop=(k == KC - 1))
                        mm.then_inc(in_ready[j], 1)
            for j in range(4):
                pe.wait_ge(in_taken[j], IN_BLOCKS + 1)
            pe.wait_ge(pool_done, 1)
            for g in range(2):
                for k in range(4):
                    mm = turn(ps[0:BUF + TS, g, k * P:(k + 1) * P], u_tail[:, 4 * g + k, :])
                mm.then_inc(tail_turned, 1)
            for g in range(12):
                c4, t = g // 3, g % 3
                t0, n = TILES[t]
                if g >= 4:
                    pe.wait_ge(v_copied, g - 3)
                for k in range(4):
                    mm = turn(ps[0:n, 4 + g % 4, k * P:(k + 1) * P], projT[:, V0 + 4 * c4 + k, t0:t0 + n])
                mm.then_inc(v_turned, 1)
            pe.wait_ge(k_rotated, 1)
            for g in range(4):
                t, hp = g // 2, g % 2
                if g >= 2:
                    pe.wait_ge(k_copied, 2 * (g - 1))
                for k in range(4):
                    mm = turn(ps[:, 2 + g % 2, k * P:(k + 1) * P], projT[:, K0 + 4 * hp + k, t * P:(t + 1) * P])
                mm.then_inc(k_turned, 1)
            pe.wait_ge(q_rotated, 1)
            pe.wait_ge(tail_copied, 2)

            def scores(h):
                if h >= 2:
                    pe.wait_ge(score_taken, 2 * (h - 1))
                for t, cols, at0 in ((0, TP, 0), (1, P, TP)):
                    for c in range(2):
                        mm = nc.tensor.matmul(ps[:, h % 2, at0:at0 + cols], projT[:, K0 + 2 * h + c, t * P:(t + 1) * P],
                                              projT[:, Q0 + 2 * h + c, TP - cols:TP], start=(c == 0), stop=(c == 1))
                mm.then_inc(scored, 1)

            scores(0)
            pe.wait_ge(v_copied, 12)
            pe.wait_ge(k_copied, 8)
            for h in range(HEADS):
                if h + 1 < HEADS:
                    scores(h + 1)
                pe.wait_ge(score_taken, 2 * (h + 1))
                for c in range(4):
                    n = 4 * h + c
                    if n >= 2:
                        pe.wait_ge(o_taken, n - 1)
                    cols = slice(h * VD + c * P, h * VD + (c + 1) * P)
                    nc.tensor.matmul(ps[:, 4 + n % 2, 0:TP], vtok[:, 0, cols], scoresT[:, h % 2, 0:TP], start=True, stop=True)
                    nc.tensor.matmul(ps[:, 4 + n % 2, P:TP], vtok[:, 1, cols], scoresT[:, h % 2, TP:TP + P],
                                     start=False, stop=True, skip_group_check=True).then_inc(o_ready, 1)
                for c in range(2):
                    n = 2 * h + c
                    if n >= 2:
                        pe.wait_ge(state_taken, n - 1)
                    for t in range(2):
                        mm = nc.tensor.matmul(ps[:, 6 + n % 2, :], kdec[:, t, (2 * h + c) * P:(2 * h + c + 1) * P],
                                              vtok[:, t, h * VD:(h + 1) * VD], start=(t == 0), stop=(t == 1))
                    mm.then_inc(state_ready, 1)

            def spread(n):
                b, h = n // HEADS, n % HEADS
                if n >= 2:
                    pe.wait_ge(outer_ready, 2 * (n - 1))
                nc.tensor.matmul(ps[:, 4 + n % 2, :], const("sel", TS)[:, b * P:(b + 1) * P], vtok[0:TS, 2, h * VD:(h + 1) * VD],
                                 start=True, stop=True).then_inc(v_spread, 1)

            pe.wait_ge(o_taken, 16)
            pe.wait_ge(mask_ready, 1)
            spread(0)
            for n in range(TS * HEADS):
                b, h = n // HEADS, n % HEADS
                if n + 1 < TS * HEADS:
                    spread(n + 1)
                pe.wait_ge(s_updated, n + 1)
                for c in range(2):
                    mm = nc.tensor.matmul(ps[0:TS, h, :], q_mask[:, 2 * h + c, b, :], ring[b % RING][:, 2 * h + c, :],
                                          start=(b == 0 and c == 0), stop=(b == TS - 1 and c == 1))
                mm.then_inc(so_done, 1)
            nslot = [(TS + j) % RING for j in range(9)]
            nload = [16 * ((ADA_BLOCKS + IN_BLOCKS) // RING + (TS + j) // RING + 1) for j in range(9)]
            pe.wait_ge(loaded[nslot[0]], nload[0])
            pe.wait_ge(pooled_s, 1)
            pe.wait_ge(so_rows, 4)
            wp = ring[nslot[0]][:].rearrange("p k n -> p (k n)")[:, 0:KC * POOL_GW].rearrange("p (k n) -> p k n", n=POOL_GW)
            for n in range(KC):
                g, c = n // 2, n % 2
                if n >= 4:
                    pe.wait_ge(mix_taken, n - 3)
                for k in range(2):
                    mm = nc.tensor.matmul(ps[:, n % 4, 0:T], wp[:, 2 * g + k, c * P:(c + 1) * P], projT[:, U0 + 2 * g + k, :], start=(k == 0), stop=(k == 1))
                mm.then_inc(mix_ready, 1)
            pe.wait_ge(state_taken, 8)
            for c in range(16):
                mm = turn(ps[:, 6, c * TS:(c + 1) * TS], o_rows[:, c * P:(c + 1) * P])
            mm.then_inc(so_turned, 1)
            pe.wait_ge(outer_ready, 2 * TS * HEADS)
            pe.wait_ge(so_copied, 1)
            for h in range(HEADS):
                for c in range(4):
                    pe.wait_ge(o_squared, h + 1)
                    mm = nc.tensor.matmul(ps[:, 4 + h, 0:T], ones, o_sq[:, c, :], start=(c == 0), stop=(c == 3))
                mm.then_inc(o_summed, 1)
            pe.wait_ge(mix_taken, KC)
            pe.wait_ge(o_normed, 1)
            for j in range(2):
                for i in range(3):
                    pe.wait_ge(loaded[nslot[1 + 3 * j + i]], nload[1 + 3 * j + i])
                a, b0, b1 = (ring[nslot[1 + 3 * j + i]] for i in range(3))
                for m in range(4):
                    n = 4 * j + m
                    if n >= 2:
                        pe.wait_ge(up_taken, n - 1)
                    ba = 2 * (n % 2)
                    for k in range(KC):
                        nc.tensor.matmul(ps[:, ba, 0:T], a[:, k, m * P:(m + 1) * P], projT[:, Q0 + k, :], start=(k == 0), stop=(k == KC - 1))
                    for k in range(2 * KC):
                        mm = nc.tensor.matmul(ps[:, ba + 1, 0:T], (b0, b1)[k // KC][:, k % KC, m * P:(m + 1) * P], projT[:, V0 + k, :], start=(k == 0), stop=(k == 2 * KC - 1))
                    mm.then_inc(up_ready, 1)
            pe.wait_ge(up_taken, KC)
            for j in range(2):
                pe.wait_ge(loaded[nslot[7 + j]], nload[7 + j])
                for m in range(4):
                    n = 4 * j + m
                    if n >= 4:
                        pe.wait_ge(x1_ready, n - 3)
                    for k in range(KC):
                        mm = nc.tensor.matmul(ps[:, 4 + n % 4, 0:T], ring[nslot[7 + j]][:, k, m * P:(m + 1) * P], mergedT[:, k, :], start=(k == 0), stop=(k == KC - 1))
                    mm.then_inc(out_ready, 1)
            pe.wait_ge(x1_ready, KC)
            sum_squares(KC)

            def rows_of(src, turned, copied):
                for g in range(6):
                    t, half = g // 2, g % 2
                    t0, n = TILES[t]
                    if g >= 4:
                        pe.wait_ge(copied[g % 2], g // 2 - 1)
                    for k in range(4):
                        mm = turn(ps[0:n, g % 4, k * P:(k + 1) * P], src[:, 4 * half + k, t0:t0 + n])
                    mm.then_inc(turned, 1)

            rows_of(xT, x1_turned, x1_copied)
            pe.wait_ge(h_ready, 2 * (KC + 1))
            pe.wait_ge(route_in, 32)
            for t, (t0, n) in enumerate(TILES):
                for k in range(KC):
                    mm = nc.tensor.matmul(ps[0:n, 4, t * E:(t + 1) * E], h2T[:, k, t0:t0 + n], routew[:, k, :], start=(k == 0), stop=(k == KC - 1))
                mm.then_inc(logit_ready, 1)
            for c in x1_copied:
                pe.wait_ge(c, 3)
            rows_of(h2T, h2_turned, h2_copied)
            for g in range(2):
                pe.wait_ge(x1_ready, KC)
                for k in range(4):
                    mm = turn(ps[0:NB, 6 + g, k * P:(k + 1) * P], modT[:, 40 + 4 * g + k, :])
                mm.then_inc(gates_turned, 1)
            pe.wait_ge(mask_sum, 1)
            for t in range(4):
                for s in range(min(t, 2) + 1):
                    mm = nc.tensor.matmul(ps[:, 5, t * E:(t + 1) * E], const("upper") if s == t else ones, maskt[:, s, :],
                                          start=(s == 0), stop=(s == min(t, 2)))
            mm.then_inc(ranked, 1)
            pe.wait_ge(prep_ready, 3)
            for t, (t0, n) in enumerate(TILES):
                mm = turn(ps[0:E, 6, t0:t0 + n], combt[0:n, t, :])
            mm.then_inc(comb_turned, 1)

            pe.wait_ge(routes_ready, 1)
            for c in h2_copied:
                pe.wait_ge(c, 3)
            rounds = pe.value_load(rounds_i[0:1, 0:1], min_val=1, max_val=3)

            def pick(q, e):
                pe.wait_ge(picked_ready, 3 * q + 3)
                for t in range(3):
                    mm = nc.tensor.matmul(ps[:, 4, 0:3], picked[:, t, :], slot_v[:, t, bass.ds(e, 1), :].rearrange("p a b -> p (a b)"),
                                          start=(t == 0), stop=(t == 2))
                mm.then_inc(slots_ready, 1)

            def turn_gathered(q):
                pe.wait_ge(xg_loaded, 16 * q + 16)
                for g in range(2):
                    for k in range(4):
                        mm = turn(ps[:, 6 + g, k * P:(k + 1) * P], xg[:, (4 * g + k) * P:(4 * g + k + 1) * P])
                    mm.then_inc(xg_turned, 1)

            def hidden(q, s, par):
                pe.wait_ge(act_ready, 2 * q + (s // 2 + 1))
                for half in range(2):
                    j = 2 * s + half
                    pe.wait_ge(lo_ready, 8 * q + (j + 1))
                    for k in range(4 * half, 4 * half + 4):
                        hi, lo = w_hi[j % 4][:, k - 4 * half, :], w_lo[s][:, k, :]
                        nc.tensor.matmul(ps[:, s, :], xgT_hi[:, par, k, :], lo, start=(k == 0), stop=False)
                        nc.tensor.matmul(ps[:, s, :], xgT_hi[:, par, k, :], hi, start=False, stop=False)
                        mm = nc.tensor.matmul(ps[:, s, :], xgT_lo[:, par, k, :], hi, start=False, stop=False)
                    mm.then_inc(half_used, 1)
                c = (0, 2, 1, 3)[s]
                nc.tensor.matmul(ps[:, s, :], bias_sel[:, par, :], bsplit[:, c * COL:(c + 1) * COL], start=False, stop=True).then_inc(hidden_ready, 1)

            def turn_hidden(m):
                for g in range(2):
                    pe.wait_ge(act_ready, 2 * m + (g + 3))
                    for k in range(4):
                        mm = turn(ps[:, 6 + g, k * P:(k + 1) * P], act[:, g, k * P:(k + 1) * P])
                    mm.then_inc(act_turned, 1)

            def outward(m):
                pe.wait_ge(act_taken, 2 * m + 2)
                pe.wait_ge(eo_taken, 2 * m + 2)
                pe.wait_ge(slots_settled, 2 * m + 2)
                for h in range(2):
                    pe.wait_ge(moe_loaded[4 + h], 16 * m + 16)
                    for k in range(KC):
                        mm = nc.tensor.matmul(ps[:, 4 + h, :], actT[:, k, :], moe_ring[4 + h][:, k, :], start=(k == 0), stop=(k == KC - 1))
                    mm.then_inc(eo_ready, 1)

            def visit(q, e, par, first=False, last=False):
                pe.wait_ge(xg_taken, 2 * q + 2)
                pe.wait_ge(bias_sel_ready, q + 1)
                hidden(q, 0, par)
                if not last:
                    if not first:
                        pe.wait_ge(eo_taken, 2 * q)
                    pick(q + 1, e + 1)
                if not first:
                    turn_hidden(q - 1)
                hidden(q, 1, par)
                if not first:
                    if not last:
                        pe.wait_ge(slots_taken, 2 * q + 4)
                    outward(q - 1)
                if not last:
                    turn_gathered(q + 1)
                hidden(q, 2, par)
                hidden(q, 3, par)

            with pe.Fori(0, rounds) as r:
                pe.wait_ge(eo_taken, r * (2 * E) + 2)
                pick(r * E, 0)
                turn_gathered(r * E)
                visit(r * E, 0, 0, first=True)
                with pe.Fori(0, E // 2 - 1) as i:
                    visit(r * E + i * 2 + 1, i * 2 + 1, 1)
                    visit(r * E + i * 2 + 2, i * 2 + 2, 0)
                visit(r * E + (E - 1), E - 1, 1, last=True)
                turn_hidden(r * E + (E - 1))
                outward(r * E + (E - 1))
            pe.wait_ge(eo_taken, rounds * (2 * E) + 2)
            pe.wait_ge(act_taken, rounds * (2 * E))
            pe.wait_ge(act_ready, rounds * (2 * E) + 2)
            pe.wait_ge(small_in, 16 * (SMALL_LOADS + 2))
            for t, (t0, n) in enumerate(TILES):
                b = 4 * (t % 2)
                if t == 2:
                    pe.wait_ge(y_step, 1)
                for h in range(2):
                    nc.tensor.matmul(ps[0:n, b + h, :], combT[:, t0:t0 + n], b_out[:, h * COL:(h + 1) * COL], start=True, stop=True)
                    mm = nc.tensor.matmul(ps[0:n, b + 2 + h, :], const("selc", NB)[:, t0:t0 + n], gate_rows[:, h * COL:(h + 1) * COL], start=True, stop=True)
                mm.then_inc(bo_ready, 1)

        @block.scalar
        def _(act_e):
            def load(dst, src):
                act_e.dma_start(dst, src).then_inc(small_in, 16)

            act_e.dma_start(ct[:], consts).then_inc(const_in, 16)
            load(xtok[:, 0:2, :], x_prompt[0].rearrange("(t p) d -> p t d", p=P))
            load(xtok[0:TS, 2, :], x_sample[:, 0])
            load(rows72[0:48], b_ada[0].rearrange("(a p) -> a p", p=P))
            load(rows72[48:56], norm1_g[0].rearrange("(a p) -> a p", p=P))
            load(rows72[56:64], norm2_g[0].rearrange("(a p) -> a p", p=P))
            load(rows72[64:72], pool_scale[0].rearrange("(a p) -> a p", p=P))
            load(crow[0:1], c_prompt)
            load(crow[1:NB], c_sample)
            load(spool[:], state_pool[0].rearrange("b t d -> (b t) d"))
            act_e.wait_ge(small_in, 16 * SMALL_LOADS)
            nc.scalar.activation(csil[:], crow[:], ACT.Silu).then_inc(c_silu, 1)
            for k in range(KC):
                act_e.wait_ge(x_turned, k + 1)
                nc.scalar.copy(xT[:, k, :], ps[:, k % 2, 0:T]).then_inc(x_copied, 1)
            for g in range(2):
                act_e.wait_ge(pool_turned, g + 1)
                for k in range(4):
                    mv = nc.scalar.copy(extS[:, 4 * g + k, :, 0:BUF], ps[:, 2 + g, k * 120:(k + 1) * 120].rearrange("p (b t) -> p b t", t=BUF))
                mv.then_inc(pool_copied, 1)

            def squares(base):
                for k in range(KC):
                    if k >= 2:
                        act_e.wait_ge(sq_summed, base + k - 1)
                    nc.scalar.activation(sq[:, k % 2, :], xT[:, k, :], ACT.Square).then_inc(sq_ready, 1)
                act_e.wait_ge(var_ready, base // KC + 1)
                nc.scalar.activation(rstd[:], rstd[:], ACT.Sqrt).then_inc(std_ready, 1)

            def modulate(h, scale, shift0, count):
                act_e.wait_ge(normed, count)
                for k in range(KC):
                    nc.scalar.activation(h[:, k, 0:TP], h[:, k, 0:TP], ACT.Identity, bias=modT[:, shift0 + k, 0:1],
                                         scale=scale[:, k, 0:1]).then_inc(h_ready, 1)

            act_e.wait_ge(x_copied, KC)
            squares(0)
            modulate(hT, scale1, 0, 1)
            for j in (0, 2):
                act_e.sem_inc(in_taken[j], 1)
            with act_e.Fori(0, IN_BLOCKS // RING) as i:
                for s in range(RING):
                    for j in (0, 2):
                        act_e.wait_ge(in_ready[j], i * RING + (s + 1))
                        nc.scalar.copy(projT[:, bass.ds((i * RING + s) * 4 + j, 1), :].rearrange("p a t -> p (a t)"), ps[:, j, 0:T]).then_inc(in_taken[j], 1)
            act_e.wait_ge(pool_done, 1)
            for g in range(12):
                c4, t = g // 3, g % 3
                n = TILES[t][1]
                act_e.wait_ge(v_turned, g + 1)
                nc.scalar.copy(vtok[0:n, t, c4 * COL:(c4 + 1) * COL], ps[0:n, 4 + g % 4, :]).then_inc(v_copied, 1)
            for j in range(4):
                act_e.wait_ge(in_taken[j], IN_BLOCKS + 1)
            nc.scalar.activation(projT[:, G0:G0 + 16, :], projT[:, G0:G0 + 16, :], ACT.Silu).then_inc(gates_ready, 1)
            nc.scalar.activation(projT[:, GA0:GA0 + 16, :], projT[:, GA0:GA0 + 16, :], ACT.Sigmoid).then_inc(gates_ready, 1)
            act_e.wait_ge(q_rotated, 1)
            for g in range(4):
                t, hp = g // 2, g % 2
                act_e.wait_ge(k_turned, g + 1)
                for h in (2 * hp, 2 * hp + 1):
                    nc.scalar.activation(kdec[:, t, h * QK:(h + 1) * QK], ps[:, 2 + g % 2, (h % 2) * QK:(h % 2 + 1) * QK], ACT.Copy,
                                         scale=const("kdecay")[:, t * HEADS + h:t * HEADS + h + 1]).then_inc(k_copied, 1)
            for h in range(HEADS):
                for c in range(4):
                    n = 4 * h + c
                    act_e.wait_ge(o_ready, n + 1)
                    nc.scalar.copy(projT[:, V0 + n, 0:TP], ps[:, 4 + n % 2, 0:TP]).then_inc(o_taken, 1)
                if h >= 1:
                    for n in (2 * h - 2, 2 * h - 1):
                        act_e.wait_ge(state_taken, n + 1)
                        act_e.dma_start(new_ret_prompt[0, 0, n // 2, (n % 2) * P:(n % 2 + 1) * P], s_stage[:, n % 2, :]).then_inc(state_stored[n % 2], 16)
            for n in (6, 7):
                act_e.wait_ge(state_taken, n + 1)
                act_e.dma_start(new_ret_prompt[0, 0, n // 2, (n % 2) * P:(n % 2 + 1) * P], s_stage[:, n % 2, :]).then_inc(state_stored[n % 2], 16)
            act_e.wait_ge(pooled_s, 1)
            act_e.wait_ge(tail_stored, 48)
            for n in range(TS * HEADS):
                b, h = n // HEADS, n % HEADS
                act_e.wait_ge(v_spread, n + 1)
                if n >= 2:
                    act_e.wait_ge(s_updated, n - 1)
                for c in range(2):
                    nc.scalar.activation(outer[:, n % 2, c, :], ps[:, 4 + n % 2, :], ACT.Copy,
                                         scale=projT[:, K0 + 2 * h + c, TP + b:TP + b + 1]).then_inc(outer_ready, 1)
            for n in range(KC):
                act_e.wait_ge(mix_ready, n + 1)
                nc.scalar.activation(projT[:, Q0 + n, :], ps[:, n % 4, 0:T], ACT.Copy, scale=vecT[:, 64 + n:65 + n]).then_inc(mix_taken, 1)
            act_e.wait_ge(so_copied, 1)
            for h in range(HEADS):
                if h >= 1:
                    act_e.wait_ge(o_summed, h)
                nc.scalar.activation(o_sq[:], projT[:, V0 + 4 * h:V0 + 4 * h + 4, :], ACT.Square).then_inc(o_squared, 1)
            act_e.wait_ge(o_var, 1)
            nc.scalar.activation(o_sq[:], o_sq[:], ACT.Sqrt).then_inc(o_std, 1)
            act_e.wait_ge(x1_ready, KC)
            act_e.dma_start(routew[:], w_router[0].rearrange("(k p) e -> p k e", p=P)).then_inc(route_in, 16)
            act_e.dma_start(rbias[:], b_router.broadcast_to([P, E])).then_inc(route_in, 16)
            for i in range(3):
                act_e.dma_start(b_full[32 * i:32 * i + 32], b_expert_in[0]).then_inc(bias_in, 16)
            squares(KC)

            def rows_out(dst, turned, copied):
                for g in range(0, 6, 2):
                    t, half = g // 2, g % 2
                    n = TILES[t][1]
                    act_e.wait_ge(turned, g + 1)
                    nc.scalar.copy(dst[0:n, t, half * COL:(half + 1) * COL], ps[0:n, g % 4, :]).then_inc(copied[0], 1)

            rows_out(rows, x1_turned, x1_copied)
            modulate(h2T, scale2, 24, 2)
            for c in x1_copied:
                act_e.wait_ge(c, 3)
            act_e.dma_start(x1_rows[0:TP].rearrange("(t p) d -> p t d", p=P), rows[:, 0:2, :]).then_inc(x1_stored, 16)
            act_e.dma_start(x1_rows[TP:T], rows[0:TS, 2, :]).then_inc(x1_stored, 16)
            act_e.wait_ge(x1_stored, 32)
            rows_out(rows, h2_turned, h2_copied)
            for c in h2_copied:
                act_e.wait_ge(c, 3)
            act_e.dma_start(h2_rows[0:TP].rearrange("(t p) d -> p t d", p=P), rows[:, 0:2, :]).then_inc(h2_stored, 16)
            act_e.dma_start(h2_rows[TP:T], rows[0:TS, 2, :]).then_inc(h2_stored, 16)
            for t, (t0, n) in enumerate(TILES):
                act_e.wait_ge(exp_in, t + 1)
                nc.scalar.activation(wk[0:n, 0:TOPK], top8[0:n, 0:TOPK], ACT.Exp, bias=small[0:n, 0:1], accum_out=small[0:n, 1:2]).then_inc(exp_out, 1)
            for g in range(2):
                act_e.wait_ge(gates_turned, g + 1)
                nc.scalar.copy(gate_rows[:, g * COL:(g + 1) * COL], ps[0:NB, 6 + g, :]).then_inc(prep_ready, 1)

            act_e.sem_inc(eo_taken, 2)
            act_e.wait_ge(h2_stored, 32)
            act_e.wait_ge(routes_ready, 1)
            rounds = act_e.value_load(rounds_i[0:1, 0:1], min_val=1, max_val=3)

            def take_gathered(q, par):
                for g in range(2):
                    act_e.wait_ge(xg_turned, 2 * q + (3 + g))
                    nc.scalar.copy(xgT_hi[:, par, 4 * g:4 * g + 4, :], ps[:, 6 + g, :].rearrange("p (k n) -> p k n", n=P)).then_inc(xg_hi, 1)

            def high(q, j):
                s, half = j // 2, j % 2
                act_e.wait_ge(moe_loaded[s], 16 * q + 16)
                act_e.wait_ge(half_used, 8 * q + (j + 1))
                nc.scalar.copy(w_hi[j % 4][:], moe_ring[s][:, 4 * half:4 * half + 4, :]).then_inc(hi_ready, 1)

            def take_turned(m):
                act_e.wait_ge(act_turned, 2 * m + 1)
                act_e.wait_ge(eo_ready, 2 * m + 2)
                nc.scalar.copy(actT[:, 0:4, :], ps[:, 6, :].rearrange("p (k n) -> p k n", n=P)).then_inc(act_taken, 1)

            def weigh(m, par):
                act_e.wait_ge(eo_ready, 2 * m + 3)
                act_e.wait_ge(rows_free, m + 1)
                nc.scalar.activation(ostage[:, par, 0:COL], ps[:, 4, :], ACT.Copy, scale=slot_w[:, par, 0:1]).then_inc(eo_taken, 1)

            def sigmoid(q, hf):
                act_e.wait_ge(glu_ready, 2 * q + (hf + 1))
                act_e.wait_ge(act_ready, 2 * q + (hf + 2))
                nc.scalar.activation(glu_s[:], glu_g[:], ACT.Sigmoid, scale=ALPHA).then_inc(sig_ready, 1)

            def visit(q, par, first=False, last=False):
                if not first:
                    sigmoid(q - 1, 1)
                high(q, 3)
                if not first:
                    take_turned(q - 1)
                high(q, 4)
                high(q, 5)
                sigmoid(q, 0)
                high(q, 6)
                high(q, 7)
                if not first:
                    weigh(q - 1, 1 - par)
                if not last:
                    take_gathered(q + 1, 1 - par)
                    for j in range(3):
                        high(q + 1, j)

            with act_e.Fori(0, rounds) as r:
                high(r * E, 0)
                high(r * E, 1)
                take_gathered(r * E, 0)
                high(r * E, 2)
                visit(r * E, 0, first=True)
                with act_e.Fori(0, E // 2 - 1) as i:
                    visit(r * E + i * 2 + 1, 1)
                    visit(r * E + i * 2 + 2, 0)
                visit(r * E + (E - 1), 1, last=True)
                sigmoid(r * E + (E - 1), 1)
                take_turned(r * E + (E - 1))
                weigh(r * E + (E - 1), 1)
            act_e.wait_ge(rows_free, rounds * E + 2)
            act_e.wait_ge(hidden_ready, rounds * (4 * E) + 8)
            load(b_out[:], b_expert_out[0])
            load(g_final[:], final_norm_g.unsqueeze(0).broadcast_to([P, D]))
            for t, (t0, n) in enumerate(TILES):
                act_e.wait_ge(y_sumsq, 2 * t + 1)
                nc.scalar.activation(y_sq[0:n], y_out[t][0:n], ACT.Square, accum_out=small[0:n, 2:3]).then_inc(y_std, 1)
                act_e.wait_ge(y_sumsq, 2 * t + 2)
                nc.scalar.activation(small[0:n, 3:4], small[0:n, 3:4], ACT.Sqrt).then_inc(y_std, 1)

        @block.vector
        def _(dve):
            done = [0]

            def step(ins):
                done[0] += 1
                ins.then_inc(dve_step, 1)
                dve.wait_ge(dve_step, done[0])

            tt, ts, stt, cp = nc.vector.tensor_tensor, nc.vector.tensor_scalar, nc.vector.scalar_tensor_tensor, nc.vector.tensor_copy
            dve.wait_ge(vec_turned, 1)
            cp(vecT[:], ps[:, 6, 0:72]).then_inc(vec_copied, 1)
            dve.wait_ge(c_turned, 1)
            cp(cT[:], ps[:, 7, 0:KC * NB].rearrange("p (k n) -> p k n", n=NB)).then_inc(c_copied, 1)

            def norm(h, base):
                dve.wait_ge(sq_summed, base + KC)
                ts(rstd[:], ps[:, 6, 0:T], 1.0 / D, EPS, ALU.mult, ALU.add).then_inc(var_ready, 1)
                dve.wait_ge(std_ready, base // KC + 1)
                step(nc.vector.reciprocal(rstd[:], rstd[:]))
                step(tt(h[:], xT[:], over(rstd[:], KC), ALU.mult))

            def modulate_samples(h, scale, shift0):
                step(tt(h[:, :, TP:T], h[:, :, TP:T], scale[:, :, 1:NB], ALU.mult))
                tt(h[:, :, TP:T], h[:, :, TP:T], modT[:, shift0:shift0 + KC, 1:NB], ALU.add).then_inc(h_ready, 1)

            dve.wait_ge(pool_turned, 2)
            dve.wait_ge(x_copied, KC)
            norm(hT, 0)
            dve.sem_inc(mod_ready, 3)
            dve.wait_ge(vec_copied, 1)
            with dve.Fori(0, ADA_BLOCKS // RING) as i:
                for s in range(RING):
                    dve.wait_ge(ada_ready, i * RING + (s + 4))
                    cp(mod_stage[:, s, :], ps[0:NB, s, :]).then_inc(ada_staged, 1)
                for s in range(RING):
                    dve.wait_ge(ada_turned, i * RING + (s + 1))
                    tt(modT[:, bass.ds((i * RING + s) * 4, 4), :], ps[:, 3 + s, 0:4 * NB].rearrange("p (k n) -> p k n", n=NB),
                       each(vecT[:, bass.ds((i * RING + s) * 4, 4)], NB), ALU.add).then_inc(mod_ready, 1)
            dve.wait_ge(mod_ready, ADA_BLOCKS + 3)
            stt(scale1[:], modT[:, 8:16, :], 1.0, each(vecT[:, 48:56], NB), ALU.add, ALU.mult).then_inc(normed, 1)
            step(stt(scale2[:], modT[:, 32:40, :], 1.0, each(vecT[:, 56:64], NB), ALU.add, ALU.mult))
            dve.wait_ge(normed, 1)
            modulate_samples(hT, scale1, 0)
            for j in (1, 3):
                dve.sem_inc(in_taken[j], 1)
            with dve.Fori(0, IN_BLOCKS // RING) as i:
                for s in range(RING):
                    for j in (1, 3):
                        dve.wait_ge(in_ready[j], i * RING + (s + 1))
                        cp(projT[:, bass.ds((i * RING + s) * 4 + j, 1), :].rearrange("p a t -> p (a t)"), ps[:, j, 0:T]).then_inc(in_taken[j], 1)
            for j in range(4):
                dve.wait_ge(in_taken[j], IN_BLOCKS + 1)
            for g in range(2):
                dve.wait_ge(tail_turned, g + 1)
                cp(u_rows[:, g * COL:(g + 1) * COL], ps[0:BUF + TS, g, :]).then_inc(tail_copied, 1)

            def rotate(first, scale, rotated):
                v = projT[:, first:first + KC, :].rearrange("p (h c) t -> p h c t", c=2)
                x1, x2 = v[:, :, 0, :], v[:, :, 1, :]
                cos, sin = over(const("cos"), HEADS), over(const("sin"), HEADS)
                stt(rot_a[:], x2, scale, sin, ALU.mult, ALU.mult).then_inc(dve_step, 1)
                stt(rot_b[:], x1, scale, sin, ALU.mult, ALU.mult).then_inc(dve_step, 1)
                done[0] += 2
                dve.wait_ge(dve_step, done[0])
                stt(x1, x1, scale, cos, ALU.mult, ALU.mult).then_inc(dve_step, 1)
                stt(x2, x2, scale, cos, ALU.mult, ALU.mult).then_inc(dve_step, 1)
                done[0] += 2
                dve.wait_ge(dve_step, done[0])
                tt(x1, x1, rot_a[:], ALU.subtract).then_inc(dve_step, 1)
                tt(x2, x2, rot_b[:], ALU.add).then_inc(dve_step, 1)
                done[0] += 2
                dve.wait_ge(dve_step, done[0])
                dve.sem_inc(rotated, 1)

            rotate(K0, float(QK) ** -0.5, k_rotated)
            rotate(Q0, 1.0, q_rotated)
            tt(q_mask[:],
               projT[:, Q0:Q0 + KC, TP:T].unsqueeze(3).broadcast_to([P, KC, TS, TS]),
               const("eye8").rearrange("p (a b) -> p a b", b=TS).unsqueeze(1).broadcast_to([P, KC, TS, TS]), ALU.mult).then_inc(mask_ready, 1)
            dve.wait_ge(pool_done, 1)
            for g, w in enumerate(WINDOWS):
                sums = outer_sum[:, 2 * g:2 * g + 2, :]
                step(nc.vector.tensor_reduce(sums, extS[:, 2 * g:2 * g + 2, :, 16 - w:16], AX, ALU.add))
                ins = stt(projT[:, U0 + 2 * g:U0 + 2 * g + 2, TP:T], sums, 1.0 / w, projT[:, U0 + 2 * g:U0 + 2 * g + 2, TP:T], ALU.mult, ALU.subtract)
                step(ins)
            dve.sem_inc(pooled_s, 1)

            def take_scores(h):
                dve.wait_ge(scored, h + 1)
                if h >= 2:
                    dve.wait_ge(o_ready, 4 * (h - 1))
                dec = const("decay")[:, h * TP:(h + 1) * TP]
                tt(scoresT[:, h % 2, 0:TP], ps[:, h % 2, 0:TP], dec, ALU.mult).then_inc(score_taken, 1)
                tt(scoresT[:, h % 2, TP:TP + P], ps[:, h % 2, TP:TP + P], dec[:, 0:P], ALU.mult).then_inc(score_taken, 1)

            take_scores(0)
            for h in range(HEADS):
                if h + 1 < HEADS:
                    take_scores(h + 1)
                for n in (2 * h, 2 * h + 1):
                    dve.wait_ge(state_ready, n + 1)
                    if n >= 2:
                        dve.wait_ge(state_stored[n % 2], 16 * (n // 2))
                    cp(s_stage[:, n % 2, :], ps[:, 6 + n % 2, :]).then_inc(state_taken, 1)
            for n in range(TS * HEADS):
                b, h = n // HEADS, n % HEADS
                if h == 0:
                    dve.wait_ge(loaded[b % RING], 16 * ((ADA_BLOCKS + IN_BLOCKS) // RING + b // RING + 1))
                dve.wait_ge(outer_ready, 2 * (n + 1))
                s = ring[b % RING][:, 2 * h:2 * h + 2, :]
                stt(s, s, GAMMA[h], outer[:, n % 2], ALU.mult, ALU.add).then_inc(s_updated, 1)
            dve.wait_ge(so_done, TS * HEADS)
            for h in range(HEADS):
                cp(o_rows[:, h * VD:(h + 1) * VD], ps[0:TS, h, :]).then_inc(so_rows, 1)
            dve.wait_ge(so_turned, 1)
            cp(projT[:, V0:V0 + 16, TP:T], ps[:, 6, 0:16 * TS].rearrange("p (c t) -> p c t", t=TS)).then_inc(so_copied, 1)
            dve.wait_ge(o_summed, HEADS)
            ts(o_sq[:], ps[:, 4:8, 0:T], 1.0 / VD, EPS, ALU.mult, ALU.add).then_inc(o_var, 1)
            dve.wait_ge(gates_ready, 2)
            step(tt(projT[:, V0:V0 + 16, :], projT[:, V0:V0 + 16, :], projT[:, G0:G0 + 16, :], ALU.mult))
            dve.wait_ge(o_std, 1)
            step(nc.vector.reciprocal(o_sq[:], o_sq[:]))
            for h in range(HEADS):
                ins = tt(projT[:, V0 + 4 * h:V0 + 4 * h + 4, :], projT[:, V0 + 4 * h:V0 + 4 * h + 4, :], over(o_sq[:, h, :], 4), ALU.mult)
                step(ins)
            dve.sem_inc(o_normed, 1)
            for n in range(KC):
                dve.wait_ge(up_ready, n + 1)
                b = 2 * (n % 2)
                step(tt(up_a[:], ps[:, b, 0:T], projT[:, GA0 + n, :], ALU.mult))
                step(tt(up_b[:], ps[:, b + 1, 0:T], projT[:, GB0 + n, :], ALU.mult))
                step(tt(mergedT[:, n, :], up_a[:], up_b[:], ALU.add))
                dve.sem_inc(up_taken, 1)
            for n in range(KC):
                dve.wait_ge(out_ready, n + 1)
                if n >= 1:
                    dve.wait_ge(x1_ready, n)
                step(tt(up_a[:, 0:TS], ps[:, 4 + n % 4, TP:T], modT[:, 16 + n, 1:NB], ALU.mult))
                step(stt(xT[:, n, 0:TP], ps[:, 4 + n % 4, 0:TP], modT[:, 16 + n, 0:1], xT[:, n, 0:TP], ALU.mult, ALU.add))
                tt(xT[:, n, TP:T], xT[:, n, TP:T], up_a[:, 0:TS], ALU.add).then_inc(x1_ready, 1)
            dve.wait_ge(x1_ready, KC)
            dve.wait_ge(bias_in, 48)
            step(cp(b_half[:], b_full[:]))
            step(cp(bsplit[0:32], b_half[0:32]))
            step(tt(b_part[:], b_full[:], b_half[:], ALU.subtract))
            step(cp(b_half[:], b_part[:]))
            step(cp(bsplit[32:64], b_half[32:64]))
            step(tt(b_full[:], b_part[:], b_half[:], ALU.subtract))
            step(cp(bsplit[64:96], b_full[64:96]))
            dve.sem_inc(prep_ready, 1)
            dve.sem_inc(bias_split, 1)

            def rows_out(dst, turned, copied):
                for g in range(1, 6, 2):
                    t, half = g // 2, g % 2
                    n = TILES[t][1]
                    dve.wait_ge(turned, g + 1)
                    cp(dst[0:n, t, half * COL:(half + 1) * COL], ps[0:n, g % 4, :]).then_inc(copied[1], 1)

            dve.wait_ge(sq_summed, 2 * KC)
            norm(h2T, KC)
            dve.sem_inc(normed, 1)
            modulate_samples(h2T, scale2, 24)
            rows_out(rows, x1_turned, x1_copied)
            dve.wait_ge(x1_stored, 32)
            rows_out(rows, h2_turned, h2_copied)
            for buf in (maskt, combt, kt):
                step(nc.vector.memset(buf[:], 0.0))
            dve.wait_ge(route_in, 32)
            for t, (t0, n) in enumerate(TILES):
                dve.wait_ge(logit_ready, 3)
                step(tt(logits[0:n], ps[0:n, 4, t * E:(t + 1) * E], rbias[0:n], ALU.add))
                step(nc.vector.max(top8[0:n], logits[0:n]))
                step(ts(small[0:n, 0:1], top8[0:n, 0:1], -1.0, None, ALU.mult))
                dve.sem_inc(exp_in, 1)
                step(nc.vector.max_index(idx8[0:n], top8[0:n], logits[0:n]))
                step(cp(idxf[0:n], idx8[0:n]))
                dve.wait_ge(exp_out, t + 1)
                step(nc.vector.reciprocal(small[0:n, 1:2], small[0:n, 1:2]))
                step(ts(wk[0:n, 0:TOPK], wk[0:n, 0:TOPK], small[0:n, 1:2], None, ALU.mult))
                for k in range(TOPK):
                    step(ts(onehot[0:n], const("iota", n)[:, 0:E], idxf[0:n, k:k + 1], None, ALU.is_equal))
                    step(tt(maskt[0:n, t], maskt[0:n, t], onehot[0:n], ALU.add))
                    step(stt(combt[0:n, t], onehot[0:n], wk[0:n, k:k + 1], combt[0:n, t], ALU.mult, ALU.add))
                    step(stt(kt[0:n, t], onehot[0:n], float(k), kt[0:n, t], ALU.mult, ALU.add))
            dve.sem_inc(mask_sum, 1)
            dve.wait_ge(ranked, 1)
            step(nc.vector.memset(rankm[:], -SKIP))
            for t in range(3):
                step(stt(rankm[:, t, 0:E], ps[:, 5, t * E:(t + 1) * E], SKIP, maskt[:, t], ALU.add, ALU.mult))
                step(ts(rankm[:, t, 0:E], rankm[:, t, 0:E], -SKIP, None, ALU.add))
                step(ts(small[:, 4:5], const("tokv")[:, t:t + 1], float(TOPK), -SKIP, ALU.mult, ALU.add))
                step(ts(slot_v[:, t, 0:E, 0], maskt[:, t], const("tokv")[:, t:t + 1], None, ALU.mult))
                step(stt(slot_v[:, t, 0:E, 1], kt[:, t], small[:, 4:5], maskt[:, t], ALU.add, ALU.mult))
                step(cp(slot_v[:, t, 0:E, 2], combt[:, t]))
            step(cp(countf[:], ps[:, 5, 3 * E:4 * E]))
            step(nc.vector.tensor_reduce(rounds_f[:, 0:1], countf[:], AX, ALU.max))
            step(ts(rounds_f[:, 1:2], rounds_f[:, 0:1], float(P), 1.0, ALU.is_gt, ALU.add))
            step(stt(rounds_f[:, 1:2], rounds_f[:, 0:1], float(2 * P), rounds_f[:, 1:2], ALU.is_gt, ALU.add))
            step(cp(rounds_i[:], rounds_f[:, 1:2]))
            dve.wait_ge(prep_ready, 3)
            dve.wait_ge(comb_turned, 1)
            step(cp(combT[:], ps[0:E, 6, 0:T]))
            dve.wait_ge(h2_stored, 32)
            dve.sem_inc(act_ready, 2)
            dve.sem_inc(routes_ready, 1)

            rounds = dve.value_load(rounds_i[0:1, 0:1], min_val=1, max_val=3)

            def choose(q, e):
                for t in range(3):
                    ts(picked[:, t, :], const("iota"), rankm[:, t, bass.ds(e, 1)], None, ALU.is_equal).then_inc(picked_ready, 1)

            def take_slots(q):
                dve.wait_ge(slots_ready, q + 1)
                cp(slot_t[:], ps[:, 4, 0:1]).then_inc(slots_taken, 1)
                cp(slot_new[:], ps[:, 4, 0:3]).then_inc(slots_taken, 1)

            def settle_slots(q, par):
                dve.wait_ge(slots_taken, 2 * q + 2)
                dve.wait_ge(rows_free, q + 1)
                ts(slot_u[:, par, :], slot_new[:, 1:2], SKIP, None, ALU.add).then_inc(slots_settled, 1)
                cp(slot_w[:, par, :], slot_new[:, 2:3]).then_inc(slots_settled, 1)
                dve.wait_ge(slots_settled, 2 * q + 2)

            def take_gathered(q, par):
                for g in range(2):
                    dve.wait_ge(xg_hi, 2 * q + (g + 1))
                    tt(xgT_lo[:, par, 4 * g:4 * g + 4, :], ps[:, 6 + g, :].rearrange("p (k n) -> p k n", n=P),
                       xgT_hi[:, par, 4 * g:4 * g + 4, :].bitcast(F32), ALU.subtract).then_inc(xg_taken, 1)

            def low(q, j):
                s, half = j // 2, j % 2
                dve.wait_ge(hi_ready, 8 * q + (j + 1))
                tt(w_lo[s][:, 4 * half:4 * half + 4, :], moe_ring[s][:, 4 * half:4 * half + 4, :], w_hi[j % 4][:].bitcast(F32),
                   ALU.subtract).then_inc(lo_ready, 1)

            def take_turned(m):
                dve.wait_ge(act_turned, 2 * m + 2)
                dve.wait_ge(eo_ready, 2 * m + 2)
                cp(actT[:, 4:8, :], ps[:, 7, :].rearrange("p (k n) -> p k n", n=P)).then_inc(act_taken, 1)

            def weigh(m, par):
                dve.wait_ge(eo_ready, 2 * m + 4)
                dve.wait_ge(rows_free, m + 1)
                ts(ostage[:, par, COL:D], ps[:, 5, :], slot_w[:, par, 0:1], None, ALU.mult).then_inc(eo_taken, 1)

            def swiglu(q, hf):
                b = 2 * hf
                dve.wait_ge(hidden_ready, 4 * q + (2 * hf + 10))
                ts(glu_g[:], ps[:, b, :], LIMIT, None, ALU.min).then_inc(glu_ready, 1)
                dve.wait_ge(act_ready, 2 * q + (hf + 2))
                ts(glu_l[:], ps[:, b + 1, :], LIMIT, -LIMIT, ALU.min, ALU.max).then_inc(moe_step, 1)
                dve.wait_ge(glu_ready, 2 * q + (hf + 1))
                dve.wait_ge(moe_step, 4 * q + (2 * hf + 1))
                stt(glu_l[:], glu_l[:], 1.0, glu_g[:], ALU.add, ALU.mult).then_inc(moe_step, 1)
                dve.wait_ge(moe_step, 4 * q + (2 * hf + 2))
                dve.wait_ge(sig_ready, 2 * q + (hf + 1))
                tt(act[:, hf, :], glu_l[:], glu_s[:], ALU.mult).then_inc(act_ready, 1)

            def visit(q, e, par, first=False, last=False):
                if not first:
                    swiglu(q - 1, 1)
                if not last:
                    choose(q + 1, e + 1)
                low(q, 2)
                low(q, 3)
                if not first:
                    take_turned(q - 1)
                settle_slots(q, par)
                if not last:
                    take_slots(q + 1)
                low(q, 4)
                low(q, 5)
                swiglu(q, 0)
                low(q, 6)
                low(q, 7)
                if not first:
                    weigh(q - 1, 1 - par)
                if not last:
                    take_gathered(q + 1, 1 - par)
                    low(q + 1, 0)
                    low(q + 1, 1)

            with dve.Fori(0, rounds) as r:
                choose(r * E, 0)
                take_slots(r * E)
                low(r * E, 0)
                low(r * E, 1)
                take_gathered(r * E, 0)
                visit(r * E, 0, 0, first=True)
                with dve.Fori(0, E // 2 - 1) as i:
                    visit(r * E + i * 2 + 1, i * 2 + 1, 1)
                    visit(r * E + i * 2 + 2, i * 2 + 2, 0)
                visit(r * E + (E - 1), E - 1, 1, last=True)
                swiglu(r * E + (E - 1), 1)
                take_turned(r * E + (E - 1))
                weigh(r * E + (E - 1), 1)
                ts(rankm[:], rankm[:], -float(P), None, ALU.add).then_inc(rank_step, 1)
                dve.wait_ge(rank_step, r + 1)

            dve.wait_ge(small_in, 16 * (SMALL_LOADS + 2))
            dve.wait_ge(rows_in, 80)
            for t, (t0, n) in enumerate(TILES):
                y = y_out[t][0:n]
                r4 = ring[t][0:n].rearrange("p k n -> p (k n)")
                step(tt(y, r4[:, 0:D], r4[:, D:2 * D], ALU.add))
                step(tt(y, y, r4[:, 2 * D:3 * D], ALU.add))
                step(tt(y, y, r4[:, 3 * D:4 * D], ALU.add))
                dve.wait_ge(bo_ready, t + 1)
                b = 4 * (t % 2)
                flat = ps[0:n, b:b + 4, :].rearrange("p b n -> p (b n)")
                step(tt(y, y, flat[:, 0:D], ALU.add))
                step(tt(y, y, flat[:, D:2 * D], ALU.mult))
                if t == 0:
                    dve.sem_inc(y_step, 1)
                step(tt(y, y, x1_rows_in[0:n, t, :], ALU.add))
                dve.sem_inc(y_sumsq, 1)
                dve.wait_ge(y_std, 2 * t + 1)
                step(ts(small[0:n, 3:4], small[0:n, 2:3], 1.0 / D, EPS, ALU.mult, ALU.add))
                dve.sem_inc(y_sumsq, 1)
                dve.wait_ge(y_std, 2 * t + 2)
                step(nc.vector.reciprocal(small[0:n, 3:4], small[0:n, 3:4]))
                step(stt(y, y, small[0:n, 3:4], g_final[0:n], ALU.mult, ALU.mult))
                dve.sem_inc(y_ready, 1)

        @block.gpsimd
        def _(pool):
            done = [0]

            def step(ins):
                done[0] += 1
                ins.then_inc(pool_step, 1)
                pool.wait_ge(pool_step, done[0])

            tt, ts, cp = nc.gpsimd.tensor_tensor, nc.gpsimd.tensor_scalar, nc.gpsimd.tensor_copy
            pool.wait_ge(h_ready, KC + 1)
            step(nc.gpsimd.memset(ext[:, :, 0:PAD], 0.0))
            for j in range(4):
                pool.wait_ge(in_taken[j], 3)
            step(cp(ext[:, :, PAD:EXT], projT[:, U0:U0 + KC, 0:TP]))
            step(cp(u_tail[:], projT[:, U0:U0 + KC, T - BUF - TS:T]))
            step(cp(extS[:, :, :, BUF], projT[:, U0:U0 + KC, TP:T]))
            step(tt(sum2[:, :, 1:EXT], ext[:, :, 1:EXT], ext[:, :, 0:EXT - 1], ALU.add))
            step(tt(sum4[:, :, 3:EXT], sum2[:, 2:8, 3:EXT], sum2[:, 2:8, 1:EXT - 2], ALU.add))
            step(tt(sum2[:, 4:8, 7:EXT], sum4[:, 2:6, 7:EXT], sum4[:, 2:6, 3:EXT - 4], ALU.add))
            step(tt(sum4[:, 4:6, 15:EXT], sum2[:, 6:8, 15:EXT], sum2[:, 6:8, 7:EXT - 8], ALU.add))
            for g, sums in enumerate((sum2[:, 0:2], sum4[:, 0:2], sum2[:, 4:6], sum4[:, 4:6])):
                w = sums[:, :, PAD:EXT]
                step(tt(w, w, over(const("cntinv")[:, g * TP:(g + 1) * TP], 2), ALU.mult))
                step(tt(projT[:, U0 + 2 * g:U0 + 2 * g + 2, 0:TP], w, ext[:, 2 * g:2 * g + 2, PAD:EXT], ALU.subtract))
            pool.sem_inc(pool_done, 1)
            pool.dma_start(new_pool_sample[0, :, 0:BUF - 1], state_pool[0, :, 1:BUF]).then_inc(tail_stored, 16)
            pool.wait_ge(tail_copied, 2)
            pool.dma_start(new_pool_prompt[0, 0], u_rows[0:BUF]).then_inc(tail_stored, 16)
            pool.dma_start(new_pool_sample[0, :, BUF - 1], u_rows[BUF:BUF + TS]).then_inc(tail_stored, 16)
            for b in range(TS):
                pool.wait_ge(s_updated, HEADS * (b + 1))
                pool.dma_start(new_ret_sample[0, b].rearrange("h (c p) v -> p (h c) v", p=P), ring[b % RING][:]).then_inc(s_stored[b % RING], 16)

            pool.sem_inc(rows_free, 2)
            pool.wait_ge(routes_ready, 1)
            rounds = pool.value_load(rounds_i[0:1, 0:1], min_val=1, max_val=3)

            def pace():
                pool.sem_inc(pool_pace, 1)

            def bias_column(q, e, par):
                pool.wait_ge(hidden_ready, 4 * q + 4)
                pace()
                cp(bias_sel[:, par, :], const("eye96", 96)[:, bass.ds(e, 1)].broadcast_to([96, P])).then_inc(bias_sel_ready, 1)

            def gather(q):
                pool.wait_ge(slots_taken, 2 * q + 2)
                pool.wait_ge(xg_turned, 2 * q + 2)
                pace()
                pool.indirect_dma_start(out=xg[:], out_offset=None, in_=h2_rows,
                                        in_offset=bass.IndirectOffsetOnAxis(ap=slot_t[:, 0:1], axis=0),
                                        bounds_check=T - 1, oob_is_err=False).then_inc(xg_loaded, 16)

            def scatter(m, par):
                pool.wait_ge(eo_taken, 2 * m + 4)
                pace()
                pool.indirect_dma_start(out=expert_rows, out_offset=bass.IndirectOffsetOnAxis(ap=slot_u[:, par, 0:1], axis=0),
                                        in_=ostage[:, par, :], in_offset=None,
                                        bounds_check=T * TOPK - 1, oob_is_err=False).then_inc(eo_stored, 16)

            def scattered(m):
                pool.wait_ge(eo_stored, 16 * m + 16)
                pool.sem_inc(rows_free, 1)

            def visit(q, e, par, first=False, last=False):
                if not last:
                    bias_column(q + 1, e + 1, 1 - par)
                    gather(q + 1)
                if not first:
                    scatter(q - 1, 1 - par)
                    scattered(q - 1)

            with pool.Fori(0, rounds) as r:
                bias_column(r * E, 0, 0)
                gather(r * E)
                visit(r * E, 0, 0, first=True)
                with pool.Fori(0, E // 2 - 1) as i:
                    visit(r * E + i * 2 + 1, i * 2 + 1, 1)
                    visit(r * E + i * 2 + 2, i * 2 + 2, 0)
                visit(r * E + (E - 1), E - 1, 1, last=True)
                scatter(r * E + (E - 1), 1)
                scattered(r * E + (E - 1))


_INS = ["x_prompt", "x_sample", "c_prompt", "c_sample", "state_pool", "state_ret", "w_ada", "b_ada", "norm1_g", "w_in",
        "w_pool", "pool_scale", "w_up_pool", "w_up_ret", "w_out", "norm2_g", "w_router", "b_router", "w_expert_in",
        "b_expert_in", "w_expert_out", "b_expert_out", "final_norm_g"]
_OUTS = [(1, TP, D), (TS, 1, D), (1, 1, BUF, D), (1, 1, HEADS, QK, VD), (1, TS, BUF, D), (1, TS, HEADS, QK, VD)]


def kernel(**inputs):
    import numpy as _np
    import concourse.bacc as _bacc
    from concourse import mybir as _mybir
    from concourse.bass_utils import run_bass_kernel_spmd as _run

    nc = _bacc.Bacc("TRN2", target_bir_lowering=False, num_devices=1)
    arrays, args = {}, []
    for name, a in [(n, inputs[n]) for n in _INS] + [("consts", constant_table())]:
        a = _np.ascontiguousarray(a)
        arrays[f"in_{name}_dram"] = a
        args.append(nc.dram_tensor(f"in_{name}_dram", a.shape, _mybir.dt.from_np(a.dtype), kind="ExternalInput").ap())
    for i, shape in enumerate(_OUTS):
        args.append(nc.dram_tensor(f"out_{i}_dram", shape, F32, kind="ExternalOutput").ap())
    trunk_kernel(nc, *args)
    r = _run(nc, [arrays], core_ids=[0])
    return tuple(r.results[0][f"out_{i}_dram"] for i in range(len(_OUTS)))
```
